# Optimizing a Trainium2 kernel written in Bass

```python
import jax, jax.numpy as jnp
from jax import lax
import numpy as np

D_MODEL = 1024
BATCH = 1
SEQ = 512
DEPTH = 2

N_MIXERS = 2
N_CONV_LAYERS = (DEPTH + 1) // 2
N_ATTN_LAYERS = DEPTH // 2
CONV_WIDTH = 3
N_HEADS = 16
HEAD_DIM = D_MODEL // N_HEADS
GRID_W = 64
WIN_H_MAX = 8
WIN_W = 16
D_FF = 4 * D_MODEL
NORM_EPS = 1e-6

kernel_name = "hybrid_shortconv_natten2d_encoder"

def rmsnorm(x, g):
    xf = x.astype(jnp.float32)
    y = xf * lax.rsqrt(jnp.mean(xf * xf, axis=-1, keepdims=True) + NORM_EPS)
    return (y * g.astype(jnp.float32)).astype(x.dtype)

def short_conv_mixer(h, w_in, conv_w, w_out):
    u = h @ w_in
    gate_b, gate_c, v = jnp.split(u, 3, axis=-1)
    z = gate_c * v
    zp = jnp.pad(z, ((0, 0), (1, 1), (0, 0)))
    zc = conv_w[0] * zp[:, :-2] + conv_w[1] * zp[:, 1:-1] + conv_w[2] * zp[:, 2:]
    return (gate_b * zc) @ w_out

def neighborhood_attention_2d(h, w_qkv, rpb, w_o):
    bsz, seq, d = h.shape
    rows = seq // GRID_W
    kh = min(WIN_H_MAX, rows)
    qkv = (h @ w_qkv).reshape(bsz, rows, GRID_W, 3, N_HEADS, HEAD_DIM)
    q = qkv[:, :, :, 0] * (HEAD_DIM ** -0.5)
    k = qkv[:, :, :, 1]
    v = qkv[:, :, :, 2]

    cols = jnp.arange(GRID_W)
    row_start = jnp.clip(jnp.arange(rows) - kh // 2, 0, rows - kh)
    col_start = jnp.clip(cols - WIN_W // 2, 0, GRID_W - WIN_W)
    col_idx = col_start[:, None] + jnp.arange(WIN_W)[None, :]
    col_off = col_idx - cols[:, None] + (WIN_W - 1)
    rpb_cols = rpb[:, :, col_off]

    def row_block(args):
        q_row, r = args
        s = row_start[r]
        k_rows = lax.dynamic_slice_in_dim(k, s, kh, axis=1)
        v_rows = lax.dynamic_slice_in_dim(v, s, kh, axis=1)
        k_nb = k_rows[:, :, col_idx]
        v_nb = v_rows[:, :, col_idx]
        scores = jnp.einsum('bqhd,brqchd->bhqrc', q_row, k_nb).astype(jnp.float32)
        row_off = s + jnp.arange(kh) - r + (WIN_H_MAX - 1)
        bias = jnp.transpose(rpb_cols[:, row_off], (0, 2, 1, 3))
        scores = scores + bias[None].astype(jnp.float32)
        p = jax.nn.softmax(scores.reshape(bsz, N_HEADS, GRID_W, kh * WIN_W), axis=-1)
        p = p.reshape(bsz, N_HEADS, GRID_W, kh, WIN_W).astype(v.dtype)
        return jnp.einsum('bhqrc,brqchd->bqhd', p, v_nb)

    out = lax.map(row_block, (jnp.transpose(q, (1, 0, 2, 3, 4)), jnp.arange(rows)))
    out = jnp.transpose(out, (1, 0, 2, 3, 4)).reshape(bsz, seq, d)
    return out @ w_o

def sqrelu_mlp(h, w_up, w_down):
    a = jax.nn.relu(h @ w_up)
    return (a * a) @ w_down

def setup_inputs(seed: int = 0) -> dict:
    key = jax.random.key(seed)
    ks = jax.random.split(key, 16)
    d = D_MODEL
    f32 = jnp.float32
    nrm = lambda k, shp, s: jax.random.normal(k, shp, f32) * s
    return {
        "x": nrm(ks[0], (BATCH, SEQ, d), 1.0),
        "norm_mix": 1.0 + nrm(ks[1], (DEPTH, d), 0.05),
        "conv_w_in": nrm(ks[2], (N_CONV_LAYERS, d, 3 * d), d ** -0.5),
        "conv_w": nrm(ks[3], (N_CONV_LAYERS, CONV_WIDTH, d), CONV_WIDTH ** -0.5),
        "conv_w_out": nrm(ks[4], (N_CONV_LAYERS, d, d), d ** -0.5),
        "attn_w_qkv": nrm(ks[5], (N_ATTN_LAYERS, d, 3 * d), d ** -0.5),
        "attn_rpb": nrm(ks[6], (N_ATTN_LAYERS, N_HEADS, 2 * WIN_H_MAX - 1, 2 * WIN_W - 1), 0.5),
        "attn_w_o": nrm(ks[7], (N_ATTN_LAYERS, d, d), d ** -0.5),
        "norm_mlp": 1.0 + nrm(ks[8], (DEPTH, d), 0.05),
        "mlp_w_up": nrm(ks[9], (DEPTH, d, D_FF), d ** -0.5),
        "mlp_w_down": nrm(ks[10], (DEPTH, D_FF, d), D_FF ** -0.5),
        "norm_final": 1.0 + nrm(ks[11], (d,), 0.05),
    }

def reference(x, norm_mix, conv_w_in, conv_w, conv_w_out, attn_w_qkv, attn_rpb,
              attn_w_o, norm_mlp, mlp_w_up, mlp_w_down, norm_final):
    for i in range(DEPTH):
        h = rmsnorm(x, norm_mix[i])
        j = i // N_MIXERS
        if i % N_MIXERS == 0:
            x = x + short_conv_mixer(h, conv_w_in[j], conv_w[j], conv_w_out[j])
        else:
            x = x + neighborhood_attention_2d(h, attn_w_qkv[j], attn_rpb[j], attn_w_o[j])
        h = rmsnorm(x, norm_mlp[i])
        x = x + sqrelu_mlp(h, mlp_w_up[i], mlp_w_down[i])
    return rmsnorm(x, norm_final)


_drawn_inputs = setup_inputs


def setup_inputs(seed=0):
    import zlib

    import numpy as np

    out = dict(_drawn_inputs(seed))
    spreads = {}
    factors = {}
    for name, (base, spread) in spreads.items():
        noise = np.random.default_rng([zlib.crc32(name.encode()), seed]).standard_normal(out[name].shape)
        drawn = base * np.exp(spread * noise) if base else spread * noise
        out[name] = __import__('jax').numpy.asarray(drawn.astype(out[name].dtype))
    for name, factor in factors.items():
        out[name] = (out[name] * factor).astype(out[name].dtype)
    return out
```

```python
import concourse.bass as bass
from concourse import mybir
from contextlib import ExitStack

P = 128
D = 1024
SEQ = 512
KT = D // P
HEADS = 16
HD = D // HEADS
ROWS, GW, WIN = 8, 64, 16
CHUNKS = 4
EPS = 1e-6

U_CV = 0
U_B = U_CV + 2 * KT
U_OUT = U_B + KT
U_MLP0 = U_OUT + KT
U_ATT = U_MLP0 + CHUNKS * 2 * KT
U_WO = U_ATT + 3 * KT
U_MLP1 = U_WO + KT
U_END = U_MLP1 + CHUNKS * 2 * KT
AHEAD = 2

KEYS = [(0, 23), (8, 31), (24, 31), (40, 24)]
KBLOCKS = [(0, 1), (0, 1, 2), (1, 2, 3), (2, 3)]
NBLOCKS = sum(len(b) for b in KBLOCKS)
BIAS_W = ROWS * (23 + 31 + 24)
MASKED = -1e30


def encoder(nc, x, weights, small, rpb, out):
    f32, f32r = mybir.dt.float32, mybir.dt.float32r
    ALU, ACT = mybir.AluOpType, mybir.ActivationFunctionType
    ctx = ExitStack()
    with ctx:
        def sb(name, shape, dt=f32):
            return ctx.enter_context(nc.sbuf_tensor(name, shape, dt))

        def sem(name):
            return ctx.enter_context(nc.semaphore(name))

        xs = sb("xs", [P, KT, SEQ])
        a_h = sb("a_h", [P, KT, SEQ], f32r)
        a_l = sb("a_l", [P, KT, SEQ], f32r)
        h_h = sb("h_h", [P, KT, SEQ], f32r)
        h_l = sb("h_l", [P, KT, SEQ], f32r)
        raw = [sb(f"raw{s}", [P, KT, P]) for s in range(4)]
        w_h = [sb(f"w_h{s}", [P, KT, P], f32r) for s in range(4)]
        w_l = [sb(f"w_l{s}", [P, KT, P], f32r) for s in range(4)]
        par = sb("par", [P, 8 * KT])
        bias = sb("bias", [P, HEADS, BIAS_W])
        BIAS_AT = [0, 8 * 23, 8 * 23, 8 * 54]
        ones = sb("ones", [P, P])
        ident = sb("ident", [P, P])
        squares = sb("squares", [P, 3 * SEQ])
        ssq = squares[:, 0:SEQ]
        sq = [squares[:, SEQ * (s + 1):SEQ * (s + 2)] for s in range(2)]
        head_bias = [squares[:, BIAS_W * s:BIAS_W * (s + 1)] for s in range(2)]
        rstd = sb("rstd", [P, SEQ])
        ev = [sb(f"ev{s}", [P, SEQ]) for s in range(2)]
        ev2 = [sb(f"ev2{s}", [P, SEQ]) for s in range(2)]
        var, std, nt = ev[0], ev2[0], ev2[1]
        qT, kT, vT = ev[0], ev[1], ev2[0]
        shared = sb("shared", [P, 4096 + 528])
        zc = shared[:, 0:4096].rearrange("p (m t) -> p m t", m=KT)
        zp = shared[:, 4096:4096 + 528]
        prob = [shared[:, n * 1280:(n + 1) * 1280] for n in range(2)]
        probT = [sb("probT0", [P, NBLOCKS * P]), shared[:, 2560:2560 + 1280]]
        v_sb = shared[:, 3840:3840 + 512].rearrange("p (b f) -> p b f", b=4)
        stat = sb("stat", [P, 2, 4, 4])

        dense = [ctx.enter_context(nc.psum_tensor(f"dense{b}", [P, 512], f32)) for b in range(2)]
        score = [ctx.enter_context(nc.psum_tensor(f"score{b}", [P, 512], f32)) for b in range(2)]
        tposed = [ctx.enter_context(nc.psum_tensor(f"tposed{b}", [P, 512], f32)) for b in range(3)]
        misc = ctx.enter_context(nc.psum_tensor("misc", [P, 512], f32))
        SCORE_AT = [(0, 0), (0, 184), (1, 0), (1, 248)]
        PROB_AT = [0, 2 * P + 64, 5 * P + 64, 8 * P + 64]

        scratch = nc.dram_tensor("bias_rows", [HEADS, ROWS, 31, ROWS], f32, kind="Internal").ap()

        raw_in = [sem(f"raw_in{s}") for s in range(4)]
        w_hi = sem("w_hi")
        w_split = sem("w_split")
        unit_done = sem("unit_done")
        taken = sem("taken")
        x_in = [sem(f"x_in{m}") for m in range(KT)]
        par_in = sem("par_in")
        rows_in = sem("rows_in")
        bias_in = sem("bias_in")
        sq_done = sem("sq_done")
        ssq_added = sem("ssq_added")
        ssq_zero = sem("ssq_zero")
        a_hi = sem("a_hi")
        a_ready = sem("a_ready")
        ssq_done = sem("ssq_done")
        var_ready = sem("var_ready")
        std_ready = sem("std_ready")
        y_ready = sem("y_ready")
        square_ready = sem("square_ready")
        inv_ready = sem("inv_ready")
        pads_zero = sem("pads_zero")
        h_hi = sem("h_hi")
        h_ready = sem("h_ready")
        const_ready = sem("const_ready")
        pad_zero = sem("pad_zero")
        masks = sem("masks")
        bias_ready = sem("bias_ready")
        v_ready = sem("v_ready")
        vtr_done = sem("vtr_done")
        s_done, s_free, neg_ready = (sem(n) for n in ("s_done", "s_free", "neg_ready"))
        exp_done, p_ready, t_done, pt_ready, pv_done = (
            sem(n) for n in ("exp_done", "p_ready", "t_done", "pt_ready", "pv_done"))
        out_ready = sem("out_ready")
        stored = sem("stored")
        chain = sem("chain")

        def gain(n, m):
            return par[:, n * KT + m:n * KT + m + 1]

        def tap(n, m):
            return par[:, (5 + n) * KT + m:(5 + n) * KT + m + 1]

        def landed(v, i=0, per=4):
            if per == 3:
                n = v - U_ATT
                return n % 3, 16 * (U_ATT // 4 + n // 3 + i + 1)
            if v < U_WO:
                return v % 4, 16 * (v // 4 + i + 1)
            n = v - U_WO
            before = U_ATT // 4 + (KT if n % 4 < 3 else 0)
            return n % 4, 16 * (before + n // 4 + i + 1)

        X_FINAL = [None, U_OUT, U_ATT - KT, U_WO, U_END - KT]

        block = ctx.enter_context(nc.Block())

        @block.sync
        def _(sp):
            def load(u, v, i=0, per=4):
                slot, _ = landed(v, i, per)
                if v >= 3:
                    sp.wait_ge(w_split, u - 2)
                sp.dma_start(raw[slot][:], weights[bass.ds(u, 1), :, :].rearrange("u p n -> (u p) n")
                             .rearrange("p (k n) -> p k n", k=KT)).then_inc(raw_in[slot], 16)

            sp.dma_start(par[:], small).then_inc(par_in, 16)
            sp.dma_start(xs[:, 0, :], x[0]).then_inc(x_in[0], 16)
            load(0, 0)
            for m in range(1, KT):
                sp.dma_start(xs[:, m, :], x[m]).then_inc(x_in[m], 16)
            load(1, 1)
            load(2, 2)
            for r in range(ROWS):
                sp.dma_start(scratch[:, r, :, :], rpb[:, :, 7 - r:15 - r]).then_inc(rows_in, 16)
            load(3, 3)
            sp.wait_ge(rows_in, 16 * ROWS)
            sp.wait_ge(masks, 1)
            for c in range(WIN):
                for blk in (0, 1, 3):
                    col = WIN * blk + c
                    start = min(max(col - WIN // 2, 0), GW - WIN)
                    at, first = start - KEYS[blk][0], start - col + WIN - 1
                    dst = bias[8 * c:8 * c + 8, :, BIAS_AT[blk] + 8 * at:BIAS_AT[blk] + 8 * at + 128]
                    src = scratch[:, :, first:first + WIN, :].rearrange("h r c k -> r h (c k)")
                    sp.dma_start(dst, src).then_inc(bias_in, 16)
            with sp.Fori(1, U_ATT // 4) as i:
                for s in range(4):
                    load(4 * i + s, 4 + s, i - 1)
            with sp.Fori(0, KT) as i:
                for s in range(3):
                    load(3 * i + (U_ATT + s), U_ATT + s, i, 3)
            with sp.Fori(0, (U_END - U_WO) // 4) as i:
                for s in range(4):
                    load(4 * i + (U_WO + s), U_WO + s, i)
            for m in range(KT):
                sp.wait_ge(out_ready, m + 1)
                sp.dma_start(out[m], zc[:, m, :]).then_inc(stored, 16)
            sp.wait_ge(stored, 16 * KT)

        @block.gpsimd
        def _(pool):
            pool.memset(ones[:], 1.0).then_inc(const_ready, 1)
            pool.memset(ident[:], 0.0).then_inc(const_ready, 1)
            pool.wait_ge(const_ready, 2)
            pool.affine_select(out=ident[:], in_=ident[:], compare_op=ALU.not_equal, fill=1.0, base=0,
                               pattern=[[-1, P]], channel_multiplier=1).then_inc(const_ready, 1)
            pool.memset(zp, 0.0).then_inc(pad_zero, 1)
            pool.memset(bias[:], MASKED).then_inc(masks, 1)

            def sum_squares(n):
                if n:
                    pool.wait_ge(ssq_done, n)
                if n == 3:
                    pool.wait_ge(s_free, HEADS)
                pool.memset(ssq, 0.0).then_inc(ssq_zero, 1)
                pool.wait_ge(ssq_zero, n + 1)
                for m in range(KT):
                    pool.wait_ge(sq_done, KT * n + m + 1)
                    if m:
                        pool.wait_ge(ssq_added, KT * n + m)
                    pool.tensor_tensor(ssq, ssq, sq[m % 2], ALU.add).then_inc(ssq_added, 1)

            def copy_bias(par_, head):
                pool.tensor_copy(head_bias[par_], bias[:, bass.ds(head, 1), :].rearrange("p a k -> p (a k)")
                                 ).then_inc(bias_ready, 1)

            for n in range(5):
                sum_squares(n)
                if n == 2:
                    pool.wait_ge(ssq_done, 3)
                    pool.wait_ge(bias_in, 16 * 3 * WIN)
                    copy_bias(0, 0)
                    copy_bias(1, 1)
                    with pool.Fori(1, KT) as j:
                        for par_ in range(2):
                            pool.wait_ge(s_free, 2 * j + (par_ - 1))
                            copy_bias(par_, 2 * j + par_)
                if n == 1:
                    pool.wait_ge(y_ready, KT)
                    for t in prob:
                        pool.memset(t, 0.0).then_inc(pads_zero, 1)

        def mlp_start(n):
            return U_MLP0 if n == 0 else U_MLP1

        def h_before(n):
            return KT if n == 0 else KT * (1 + CHUNKS + 1)

        @block.tensor
        def _(pe):
            def product(u, slot, bank, hi, lo, ready=None, free=1):
                pe.wait_ge(w_split, u + 1)
                if free is not None:
                    pe.wait_ge(taken, u - free)
                for k in range(KT):
                    if ready is not None:
                        pe.wait_ge(ready[0], ready[1] + (k + 1))
                    nc.tensor.matmul(dense[bank][:], w_h[slot][:, k, :], hi[:, k, :], start=k == 0, stop=False)
                    nc.tensor.matmul(dense[bank][:], w_h[slot][:, k, :], lo[:, k, :], start=False, stop=False)
                    last = nc.tensor.matmul(dense[bank][:], w_l[slot][:, k, :], hi[:, k, :], start=False,
                                            stop=k == KT - 1)
                last.then_inc(unit_done, 1)

            def sum_over_partitions(n):
                pe.wait_ge(ssq_added, KT * (n + 1))
                if n:
                    pe.wait_ge(var_ready, n)
                nc.tensor.matmul(misc[:], ones[:], ssq, start=True, stop=True).then_inc(ssq_done, 1)

            def products(first, count, hi, lo, ready, lo_i=0):
                with pe.Fori(lo_i, count // 4) as i:
                    for s in range(4):
                        product(first + 4 * i + s, s, s % 2, hi, lo, ready if s == 0 else None)

            pe.wait_ge(const_ready, 3)
            product(0, 0, 0, a_h, a_l, (a_ready, 0), None)
            sum_over_partitions(0)
            product(1, 1, 1, a_h, a_l, None, None)
            product(2, 2, 0, a_h, a_l)
            product(3, 3, 1, a_h, a_l)
            products(U_CV, 2 * KT, a_h, a_l, None, 1)
            products(U_B, KT, a_h, a_l, None)
            products(U_OUT, KT, h_h, h_l, (h_ready, 0))

            def mlp(n, norm):
                sum_over_partitions(norm)
                with pe.Fori(0, CHUNKS) as c:
                    u = mlp_start(n) + 2 * KT * c
                    products(u, KT, a_h, a_l, (a_ready, KT * norm))
                    products(u + KT, KT, h_h, h_l, (h_ready, h_before(n) + KT * c))

            mlp(0, 1)

            def scores(par_, head, pair):
                if par_ == 0:
                    pe.wait_ge(taken, 3 * pair + (U_ATT + 3))
                rows = slice(HD * par_, HD * par_ + HD)
                if head is not None:
                    pe.wait_ge(s_free, head)
                for b, (c0, nk) in enumerate(KEYS):
                    bank, at = SCORE_AT[b]
                    last = nc.tensor.matmul(score[bank][:, at:at + 8 * nk], qT[rows, P * b:P * b + P],
                                            kT[rows, 8 * c0:8 * (c0 + nk)], start=True, stop=True)
                last.then_inc(s_done, 1)

            def transposes(par_, head):
                pe.wait_ge(p_ready, head + 1)
                pe.wait_ge(pt_ready, head)
                for t in range(NBLOCKS):
                    last = nc.tensor.transpose(tposed[t // 4][:, P * (t % 4):P * (t % 4) + P],
                                               prob[par_][:, P * t:P * t + P], ident[:])
                last.then_inc(t_done, 1)

            def values(par_, head, pair):
                pe.wait_ge(pt_ready, head + 1)
                if par_ == 0:
                    pe.wait_ge(v_ready, pair + 1)
                t = 0
                rows = slice(HD * par_, HD * par_ + HD)
                for b, kb in enumerate(KBLOCKS):
                    for n, k in enumerate(kb):
                        last = nc.tensor.matmul(misc[rows, P * b:P * b + P], v_sb[:, k, rows],
                                                probT[par_][:, P * t:P * t + P], start=n == 0,
                                                stop=n == len(kb) - 1)
                        t += 1
                last.then_inc(pv_done, 1)

            def value_transposes(pair):
                pe.wait_ge(taken, 3 * pair + (U_ATT + 1))
                pe.wait_ge(h_ready, pair + KT * (1 + CHUNKS))
                for b in range(4):
                    last = nc.tensor.transpose(misc[:, P * b:P * b + P], vT[:, P * b:P * b + P], ident[:])
                last.then_inc(vtr_done, 1)

            def pair_step(pair, u):
                if u is not None:
                    product(u, 0, 0, a_h, a_l, None, 0)
                value_transposes(pair)
                scores(0, 2 * pair, pair)
                if u is not None:
                    product(u + 1, 1, 1, a_h, a_l, None, 2)
                scores(1, 2 * pair + 1, pair)
                transposes(0, 2 * pair)
                if u is not None:
                    product(u + 2, 2, 0, a_h, a_l, None, 1)
                transposes(1, 2 * pair + 1)
                values(0, 2 * pair, pair)
                values(1, 2 * pair + 1, pair)

            sum_over_partitions(2)
            pe.wait_ge(var_ready, 3)
            product(U_ATT, 0, 0, a_h, a_l, (a_ready, 2 * KT), 0)
            product(U_ATT + 1, 1, 1, a_h, a_l, None, 2)
            product(U_ATT + 2, 2, 0, a_h, a_l, None, 1)
            with pe.Fori(0, KT - 1) as j:
                pair_step(j, 3 * j + (U_ATT + 3))
            pair_step(KT - 1, None)
            pe.wait_ge(taken, U_WO)
            products(U_WO, KT, h_h, h_l, (h_ready, KT * (1 + CHUNKS)))
            mlp(1, 3)
            sum_over_partitions(4)

        @block.scalar
        def _(act):
            def split_hi(v, vc, i=0, per=4):
                slot, count = landed(vc, i, per)
                act.wait_ge(raw_in[slot], count)
                if vc >= 3:
                    act.wait_ge(unit_done, v - 2)
                nc.scalar.activation(w_h[slot][:], raw[slot][:], ACT.Copy).then_inc(w_hi, 1)

            def split_x(n, m):
                if n == 0:
                    act.wait_ge(x_in[m], 16)
                else:
                    act.wait_ge(taken, X_FINAL[n] + m + 1)
                if KT * n + m >= 2:
                    act.wait_ge(ssq_added, KT * n + m - 1)
                if n < 4:
                    nc.scalar.activation(a_h[:, m, :], xs[:, m, :], ACT.Copy, scale=gain(n, m)).then_inc(a_hi, 1)
                nc.scalar.activation(sq[m % 2], xs[:, m, :], ACT.Square).then_inc(sq_done, 1)

            def root(n):
                act.wait_ge(var_ready, n + 1)
                nc.scalar.activation(std[:], var[:], ACT.Sqrt).then_inc(std_ready, 1)

            def second_hi(m, ready, count, func):
                act.wait_ge(ready, count)
                nc.scalar.activation(h_h[:, m, :], ev[m % 2][:], func).then_inc(h_hi, 1)

            act.wait_ge(par_in, 16)
            split_x(0, 0)
            split_hi(0, 0)
            for m in range(1, KT):
                split_x(0, m)
            split_hi(1, 1)
            root(0)
            for u in range(U_CV, U_B):
                split_hi(u + AHEAD, u + AHEAD)
            for m in range(KT):
                split_hi(U_B + m + AHEAD, U_B + m + AHEAD)
                second_hi(m, y_ready, m + 1, ACT.Copy)
            for m in range(KT):
                split_hi(U_OUT + m + AHEAD, U_OUT + m + AHEAD)
                split_x(1, m)

            def mlp(n, norm):
                root(norm)

                def chunk(c, last):
                    u = mlp_start(n) + 2 * KT * c
                    i = 4 * c
                    for m in range(KT):
                        vc = mlp_start(n) + m + AHEAD
                        split_hi(u + (m + AHEAD), vc, i)
                        second_hi(m, taken, u + (m + 1), ACT.Square)
                    for m in range(KT):
                        vc = mlp_start(n) + KT + m + AHEAD
                        if not (last and n == 1 and m >= KT - AHEAD):
                            split_hi(u + (KT + m + AHEAD), vc, i)
                        if last:
                            split_x(norm + 1, m)

                with act.Fori(0, CHUNKS - 1) as c:
                    chunk(c, False)
                chunk(CHUNKS - 1, True)

            mlp(0, 1)
            root(2)

            def pair_step(pair, u):
                hi = lambda s: split_hi(u + (s + AHEAD), U_ATT + 3 + s + AHEAD, pair, 3)
                if u is not None:
                    hi(0)
                act.wait_ge(vtr_done, pair + 1)
                nc.scalar.activation(v_sb, misc[:].rearrange("p (b f) -> p b f", b=4), ACT.Copy).then_inc(v_ready, 1)

                def exps(par_):
                    head = 2 * pair + par_
                    act.wait_ge(neg_ready, head + 1)
                    for b, (c0, nk) in enumerate(KEYS):
                        t = prob[par_][:, PROB_AT[b]:PROB_AT[b] + 8 * nk]
                        last = nc.scalar.activation(t, t, ACT.Exp, bias=stat[:, par_, 1, b:b + 1],
                                                    accum_out=stat[:, par_, 2, b:b + 1])
                    last.then_inc(exp_done, 1)

                def evacuate(par_):
                    head = 2 * pair + par_
                    act.wait_ge(t_done, head + 1)
                    for b in range(3):
                        w = min(512, NBLOCKS * P - 512 * b)
                        last = nc.scalar.activation(probT[par_][:, 512 * b:512 * b + w], tposed[b][:, 0:w], ACT.Copy)
                    last.then_inc(pt_ready, 1)

                exps(0)
                if u is not None:
                    hi(1)
                evacuate(0)
                exps(1)
                if u is not None:
                    hi(2)
                evacuate(1)
                act.wait_ge(pv_done, 2 * pair + 2)
                nc.scalar.activation(h_h[:, bass.ds(pair, 1), :].rearrange("p a t -> p (a t)"), misc[:],
                                     ACT.Copy).then_inc(h_hi, 1)

            for s in range(3):
                split_hi(U_ATT + s + AHEAD, U_ATT + s + AHEAD, 0, 3)
            with act.Fori(0, KT - 1) as j:
                pair_step(j, 3 * j + (U_ATT + 3))
            pair_step(KT - 1, None)
            for m in range(KT):
                split_hi(U_WO + m + AHEAD, U_WO + m + AHEAD)
                split_x(3, m)
            mlp(1, 3)
            root(4)

        @block.vector
        def _(dve):
            steps = [0]

            def link(instruction):
                steps[0] = steps[0] + 1
                instruction.then_inc(chain, 1)
                dve.wait_ge(chain, steps[0])

            def split_lo(v, vc, i=0, per=4):
                slot, _ = landed(vc, i, per)
                dve.wait_ge(w_hi, v + 1)
                nc.vector.tensor_tensor(w_l[slot][:], raw[slot][:], w_h[slot][:].bitcast(f32),
                                        ALU.subtract).then_inc(w_split, 1)

            def split_x(n, m):
                dve.wait_ge(a_hi, KT * n + m + 1)
                nc.vector.scalar_tensor_tensor(out=a_l[:, m, :], in0=xs[:, m, :], scalar=gain(n, m),
                                               in1=a_h[:, m, :].bitcast(f32), op0=ALU.mult,
                                               op1=ALU.subtract).then_inc(a_ready, 1)

            def inverse_rms(n):
                dve.wait_ge(ssq_done, n + 1)
                nc.vector.tensor_scalar(var[:], misc[:], 1.0 / D, EPS, ALU.mult, ALU.add).then_inc(var_ready, 1)
                dve.wait_ge(std_ready, n + 1)
                link(nc.vector.reciprocal(std[:], std[:]))
                link(nc.vector.tensor_tensor(nt[:], std[:], std[:], ALU.mult))
                link(nc.vector.tensor_tensor(nt[:], nt[:], var[:], ALU.mult))
                link(nc.vector.tensor_scalar(nt[:], nt[:], -0.5, 1.5, ALU.mult, ALU.add))
                link(nc.vector.tensor_tensor(rstd[:], std[:], nt[:], ALU.mult))

            def scaled(u, bank, dst):
                dve.wait_ge(unit_done, u + 1)
                nc.vector.tensor_tensor(dst, dense[bank][:], rstd[:], ALU.mult).then_inc(taken, 1)

            def residual(u, bank, m):
                dve.wait_ge(unit_done, u + 1)
                nc.vector.tensor_tensor(xs[:, m, :], dense[bank][:], xs[:, m, :], ALU.add).then_inc(taken, 1)

            dve.wait_ge(par_in, 16)
            split_x(0, 0)
            split_lo(0, 0)
            for m in range(1, KT):
                split_x(0, m)
            split_lo(1, 1)
            inverse_rms(0)
            dve.wait_ge(pad_zero, 1)
            for m in range(KT):
                u = U_CV + 2 * m
                split_lo(u + 2, u + 2)
                scaled(u, 0, ev[0][:])
                split_lo(u + 3, u + 3)
                scaled(u + 1, 1, ev[1][:])
                dve.wait_ge(taken, u + 2)
                link(nc.vector.tensor_tensor(zp[:, 8:520], ev[0][:], ev[1][:], ALU.mult))
                nc.vector.tensor_copy(zp[:, 1:8], zp[:, 512:519])
                link(nc.vector.tensor_copy(zp[:, 520:527], zp[:, 9:16]))
                link(nc.vector.tensor_scalar(ev2[0][:], zp[:, 0:512], tap(0, m), None, ALU.mult))
                link(nc.vector.scalar_tensor_tensor(out=ev2[1][:], in0=zp[:, 8:520], scalar=tap(1, m),
                                                    in1=ev2[0][:], op0=ALU.mult, op1=ALU.add))
                link(nc.vector.scalar_tensor_tensor(out=zc[:, m, :], in0=zp[:, 16:528], scalar=tap(2, m),
                                                    in1=ev2[1][:], op0=ALU.mult, op1=ALU.add))
            for m in range(KT):
                u = U_B + m
                split_lo(u + 2, u + 2)
                scaled(u, m % 2, ev2[m % 2][:])
                dve.wait_ge(taken, u + 1)
                nc.vector.tensor_tensor(ev[m % 2][:], ev2[m % 2][:], zc[:, m, :], ALU.mult).then_inc(y_ready, 1)
                dve.wait_ge(y_ready, m + 1)
                dve.wait_ge(h_hi, m + 1)
                nc.vector.tensor_tensor(h_l[:, m, :], ev[m % 2][:], h_h[:, m, :].bitcast(f32),
                                        ALU.subtract).then_inc(h_ready, 1)
            for m in range(KT):
                u = U_OUT + m
                split_lo(u + 2, u + 2)
                residual(u, m % 2, m)
                split_x(1, m)

            def mlp(n, norm):
                inverse_rms(norm)

                def chunk(c, last):
                    u = mlp_start(n) + 2 * KT * c
                    i = 4 * c
                    for m in range(KT):
                        split_lo(u + (m + AHEAD), mlp_start(n) + m + AHEAD, i)
                        tile = h_before(n) + KT * c + (m + 1)
                        dve.wait_ge(unit_done, u + (m + 1))
                        nc.vector.scalar_tensor_tensor(out=ev[m % 2][:], in0=dense[m % 2][:], scalar=0.0,
                                                       in1=rstd[:], op0=ALU.max, op1=ALU.mult).then_inc(taken, 1)
                        dve.wait_ge(taken, u + (m + 1))
                        nc.vector.tensor_tensor(ev2[m % 2][:], ev[m % 2][:], ev[m % 2][:],
                                                ALU.mult).then_inc(square_ready, 1)
                        dve.wait_ge(square_ready, tile - (KT if n == 0 else 2 * KT))
                        dve.wait_ge(h_hi, tile)
                        nc.vector.tensor_tensor(h_l[:, m, :], ev2[m % 2][:], h_h[:, m, :].bitcast(f32),
                                                ALU.subtract).then_inc(h_ready, 1)
                    for m in range(KT):
                        if not (last and n == 1 and m >= KT - AHEAD):
                            split_lo(u + (KT + m + AHEAD), mlp_start(n) + KT + m + AHEAD, i)
                        residual(u + (KT + m), m % 2, m)
                        if last and norm < 3:
                            split_x(norm + 1, m)

                with dve.Fori(0, CHUNKS - 1) as c:
                    chunk(c, False)
                chunk(CHUNKS - 1, True)

            mlp(0, 1)

            def soft_scores(par_, head):
                dve.wait_ge(s_done, head + 1)
                dve.wait_ge(bias_ready, head + 1)
                nc.vector.memset(stat[:, par_, 2, :], 0.0)
                for b, (c0, nk) in enumerate(KEYS):
                    bank, at = SCORE_AT[b]
                    last = nc.vector.tensor_tensor_reduce(
                        out=prob[par_][:, PROB_AT[b]:PROB_AT[b] + 8 * nk], in0=score[bank][:, at:at + 8 * nk],
                        in1=head_bias[par_][:, BIAS_AT[b]:BIAS_AT[b] + 8 * nk],
                        scale=1.0, scalar=-3e38, op0=ALU.add, op1=ALU.max, accum_out=stat[:, par_, 0, b:b + 1])
                last.then_inc(s_free, 1)
                dve.wait_ge(s_free, head + 1)
                nc.vector.tensor_scalar(stat[:, par_, 1, :], stat[:, par_, 0, :], -1.0, None,
                                        ALU.mult).then_inc(neg_ready, 1)

            def normalise(par_, head):
                dve.wait_ge(exp_done, head + 1)
                nc.vector.reciprocal(stat[:, par_, 3, :], stat[:, par_, 2, :]).then_inc(inv_ready, 1)
                dve.wait_ge(inv_ready, head + 1)
                for b, (c0, nk) in enumerate(KEYS):
                    t = prob[par_][:, PROB_AT[b]:PROB_AT[b] + 8 * nk]
                    last = nc.vector.tensor_scalar(t, t, stat[:, par_, 3, b:b + 1], None, ALU.mult)
                last.then_inc(p_ready, 1)

            def take_v(u):
                scaled(u, 0, vT[:])

            def take_q(u):
                dve.wait_ge(unit_done, u + 1)
                nc.vector.scalar_tensor_tensor(out=qT[:], in0=dense[1][:], scalar=HD ** -0.5, in1=rstd[:],
                                               op0=ALU.mult, op1=ALU.mult).then_inc(taken, 1)

            def take_k(u):
                scaled(u, 0, kT[:])

            def pair_step(pair, u):
                lo = lambda s: split_lo(u + (s + AHEAD), U_ATT + 3 + s + AHEAD, pair, 3)
                if u is not None:
                    lo(0)
                    dve.wait_ge(vtr_done, pair + 1)
                    take_v(u)
                soft_scores(0, 2 * pair)
                if u is not None:
                    lo(1)
                normalise(0, 2 * pair)
                soft_scores(1, 2 * pair + 1)
                if u is not None:
                    take_q(u + 1)
                    lo(2)
                normalise(1, 2 * pair + 1)
                if u is not None:
                    take_k(u + 2)
                dve.wait_ge(h_hi, pair + (KT * (1 + CHUNKS) + 1))
                high = h_h[:, bass.ds(pair, 1), :].rearrange("p a t -> p (a t)").bitcast(f32)
                low = h_l[:, bass.ds(pair, 1), :].rearrange("p a t -> p (a t)")
                nc.vector.tensor_tensor(low, misc[:], high, ALU.subtract).then_inc(h_ready, 1)

            inverse_rms(2)
            for s, take in enumerate((take_v, take_q, take_k)):
                split_lo(U_ATT + s + AHEAD, U_ATT + s + AHEAD, 0, 3)
                take(U_ATT + s)
            dve.wait_ge(pads_zero, 2)
            with dve.Fori(0, KT - 1) as j:
                pair_step(j, 3 * j + (U_ATT + 3))
            pair_step(KT - 1, None)
            for m in range(KT):
                split_lo(U_WO + m + AHEAD, U_WO + m + AHEAD)
                residual(U_WO + m, m % 2, m)
                split_x(3, m)
            mlp(1, 3)
            inverse_rms(4)
            for m in range(KT):
                nc.vector.scalar_tensor_tensor(out=zc[:, m, :], in0=xs[:, m, :], scalar=gain(4, m), in1=rstd[:],
                                               op0=ALU.mult, op1=ALU.mult).then_inc(out_ready, 1)


def kernel(x, norm_mix, conv_w_in, conv_w, conv_w_out, attn_w_qkv, attn_rpb, attn_w_o, norm_mlp,
           mlp_w_up, mlp_w_down, norm_final):
    import numpy as np
    import concourse.bacc as bacc
    from concourse.bass_utils import run_bass_kernel_spmd

    def units(w, rows, cols):
        block = w[P * KT * rows:P * KT * (rows + 1), P * cols:P * (cols + 1)]
        return block.reshape(KT, P, P).transpose(1, 0, 2).reshape(P, KT * P)

    w_in, w_qkv = conv_w_in[0], attn_w_qkv[0]
    order = []
    for m in range(KT):
        order += [units(w_in, 0, KT + m), units(w_in, 0, 2 * KT + m)]
    order += [units(w_in, 0, m) for m in range(KT)]
    order += [units(conv_w_out[0], 0, m) for m in range(KT)]

    def mlp_units(n):
        for c in range(CHUNKS):
            yield from (units(mlp_w_up[n], 0, KT * c + m) for m in range(KT))
            yield from (units(mlp_w_down[n], c, m) for m in range(KT))

    order += mlp_units(0)
    for j in range(KT):
        order += [units(w_qkv, 0, 2 * KT + j), units(w_qkv, 0, j), units(w_qkv, 0, KT + j)]
    order += [units(attn_w_o[0], 0, m) for m in range(KT)]
    order += mlp_units(1)
    weights = np.stack(order)

    x_t = x[0].reshape(ROWS, GW, D).transpose(2, 1, 0).reshape(KT, P, SEQ)
    vectors = [norm_mix[0], norm_mlp[0], norm_mix[1], norm_mlp[1], norm_final, *conv_w[0]]
    small = np.stack(vectors).reshape(8, KT, P).transpose(2, 0, 1).reshape(P, 8 * KT)
    arrays = {"x": x_t, "weights": weights, "small": small, "rpb": attn_rpb[0].transpose(0, 2, 1)}
    arrays = {name: np.ascontiguousarray(a) for name, a in arrays.items()}

    nc = bacc.Bacc("TRN2", target_bir_lowering=False, num_devices=1)
    args = [nc.dram_tensor(name, a.shape, mybir.dt.from_np(a.dtype), kind="ExternalInput").ap()
            for name, a in arrays.items()]
    out = nc.dram_tensor("out", (KT, P, SEQ), mybir.dt.float32, kind="ExternalOutput").ap()
    encoder(nc, *args, out)
    got = run_bass_kernel_spmd(nc, [arrays], core_ids=[0]).results[0]["out"]
    return np.ascontiguousarray(got.reshape(D, GW, ROWS).transpose(2, 1, 0).reshape(1, SEQ, D))
```

```python
import concourse.bass as bass
from concourse import mybir
from contextlib import ExitStack

P = 128
D = 1024
SEQ = 512
KT = D // P
HEADS = 16
HD = D // HEADS
ROWS, GW, WIN = 8, 64, 16
CHUNKS = 4
EPS = 1e-6

U_CV = 0
U_B = U_CV + 2 * KT
U_OUT = U_B + KT
U_MLP0 = U_OUT + KT
U_ATT = U_MLP0 + CHUNKS * 2 * KT
U_WO = U_ATT + 3 * KT
U_MLP1 = U_WO + KT
U_END = U_MLP1 + CHUNKS * 2 * KT
AHEAD = 2

KEYS = [(0, 23), (8, 31), (24, 31), (40, 24)]
HALVES = [(0, 1), (2, 3)]
CHUNKS_OF = [[(ROWS * c0, P), (ROWS * c0 + P, ROWS * nk - P)] for c0, nk in KEYS]
PROB_W = max(2 * ROWS * (KEYS[a][1] + KEYS[b][1]) for a, b in HALVES)
BIAS_W = ROWS * (23 + 31 + 24)
MASKED = -1e30


def encoder(nc, x, weights, small, rpb, out):
    f32, f32r = mybir.dt.float32, mybir.dt.float32r
    ALU, ACT = mybir.AluOpType, mybir.ActivationFunctionType
    ctx = ExitStack()
    with ctx:
        def sb(name, shape, dt=f32):
            return ctx.enter_context(nc.sbuf_tensor(name, shape, dt))

        def sem(name):
            return ctx.enter_context(nc.semaphore(name))

        xs = sb("xs", [P, KT, SEQ])
        a_h = sb("a_h", [P, KT, SEQ], f32r)
        a_l = sb("a_l", [P, KT, SEQ], f32r)
        h_h = sb("h_h", [P, KT, SEQ], f32r)
        h_l = sb("h_l", [P, KT, SEQ], f32r)
        raw = [sb(f"raw{s}", [P, KT, P]) for s in range(4)]
        w_h = [sb(f"w_h{s}", [P, KT, P], f32r) for s in range(4)]
        w_l = [sb(f"w_l{s}", [P, KT, P], f32r) for s in range(4)]
        par = sb("par", [P, 8 * KT])
        bias = sb("bias", [P, HEADS, BIAS_W])
        BIAS_AT = [0, 8 * 23, 8 * 23, 8 * 54]
        ones = sb("ones", [P, P])
        ident = sb("ident", [P, P])
        squares = sb("squares", [P, 3 * SEQ])
        ssq = squares[:, 0:SEQ]
        sq = [squares[:, SEQ * (s + 1):SEQ * (s + 2)] for s in range(2)]
        head_bias = [squares[:, BIAS_W * s:BIAS_W * (s + 1)] for s in range(2)]
        rstd = sb("rstd", [P, SEQ])
        ev = [sb(f"ev{s}", [P, SEQ]) for s in range(2)]
        ev2 = [sb(f"ev2{s}", [P, SEQ]) for s in range(2)]
        diag = ev2[1]
        qT, kT, vT = ev[0], ev[1], ev2[0]
        shared = sb("shared", [P, 2 * PROB_W + 3 * 1024])
        zc = shared[:, 0:4096].rearrange("p (m t) -> p m t", m=KT)
        zp = shared[:, 4096:4096 + 528]
        prob = [shared[:, PROB_W * n:PROB_W * (n + 1)] for n in range(2)]
        probT = [shared[:, 2 * PROB_W + 1024 * n:2 * PROB_W + 1024 * (n + 1)] for n in range(2)]
        v_sb = shared[:, 2 * PROB_W + 2048:2 * PROB_W + 3072].rearrange("p (c f) -> p c f", c=8)
        tok = sb("tok", [P, 5, 4])
        stat = sb("stat", [P, 2, 4, 4])

        bank = [ctx.enter_context(nc.psum_tensor(f"bank{b}", [P, 512], f32)) for b in range(8)]
        dense = bank[0:4]
        score, tposed = bank[2:4], bank[4:6]
        vtr = bank[6:8]
        attn_out = bank[6]
        sums, spread = bank[7][:, 0:4], bank[6]

        def score_at(half, n):
            first, width = (0 if n == 0 else ROWS * KEYS[HALVES[half][0]][1]), ROWS * KEYS[HALVES[half][n]][1]
            return slice(first, first + width)

        def prob_at(half, par_, n):
            at = score_at(half, n)
            offset = par_ * PROB_W // 2
            return slice(offset + at.start, offset + at.stop)

        scratch = nc.dram_tensor("bias_rows", [HEADS, ROWS, 31, ROWS], f32, kind="Internal").ap()

        raw_in = [sem(f"raw_in{s}") for s in range(4)]
        w_hi = sem("w_hi")
        w_split = sem("w_split")
        unit_done = sem("unit_done")
        taken = sem("taken")
        x_in = [sem(f"x_in{m}") for m in range(KT)]
        par_in = sem("par_in")
        rows_in = sem("rows_in")
        bias_in = sem("bias_in")
        sq_done = sem("sq_done")
        ssq_added = sem("ssq_added")
        ssq_zero = sem("ssq_zero")
        a_hi = sem("a_hi")
        a_ready = sem("a_ready")
        ssq_done = sem("ssq_done")
        diag_ready = sem("diag_ready")
        spread_done = sem("spread_done")
        rstd_ready = sem("rstd_ready")
        piece_hi = sem("piece_hi")
        piece_split = sem("piece_split")
        var_ready = sem("var_ready")
        std_ready = sem("std_ready")
        y_ready = sem("y_ready")
        square_ready = sem("square_ready")
        banks_zero = sem("banks_zero")
        h_hi = sem("h_hi")
        h_ready = sem("h_ready")
        const_ready = sem("const_ready")
        pad_zero = sem("pad_zero")
        masks = sem("masks")
        bias_ready = sem("bias_ready")
        vtr_done = sem("vtr_done")
        v_ready = sem("v_ready")
        s_done = sem("s_done")
        s_free = sem("s_free")
        neg_ready = sem("neg_ready")
        exp_done = sem("exp_done")
        inv_ready = sem("inv_ready")
        p_ready = sem("p_ready")
        t_done = sem("t_done")
        pt_ready = sem("pt_ready")
        pt_ready_o = sem("pt_ready_o")
        pv_done = sem("pv_done")
        out_ready = sem("out_ready")
        stored = sem("stored")
        chain = sem("chain")

        def gain(n, m):
            return par[:, n * KT + m:n * KT + m + 1]

        def tap(n, m):
            return par[:, (5 + n) * KT + m:(5 + n) * KT + m + 1]

        def landed(v, i=0, per=4):
            if per == 3:
                n = v - U_ATT
                return n % 3, 16 * (U_ATT // 4 + n // 3 + i + 1)
            if v < U_WO:
                return v % 4, 16 * (v // 4 + i + 1)
            n = v - U_WO
            before = U_ATT // 4 + (KT if n % 4 < 3 else 0)
            return n % 4, 16 * (before + n // 4 + i + 1)

        X_FINAL = [None, U_OUT, U_ATT - KT, U_WO, U_END - KT]

        block = ctx.enter_context(nc.Block())

        def adds_before(n):
            return KT * n - min(n, 1)

        @block.sync
        def _(sp):
            def load(u, v, i=0, per=4):
                slot, _ = landed(v, i, per)
                if v >= 3:
                    sp.wait_ge(w_split, u - 2)
                sp.dma_start(raw[slot][:], weights[bass.ds(u, 1), :, :].rearrange("u p n -> (u p) n")
                             .rearrange("p (k n) -> p k n", k=KT)).then_inc(raw_in[slot], 16)

            sp.dma_start(par[:], small).then_inc(par_in, 16)
            sp.dma_start(xs[:, 0, :], x[0]).then_inc(x_in[0], 16)
            load(0, 0)
            for m in range(1, KT):
                sp.dma_start(xs[:, m, :], x[m]).then_inc(x_in[m], 16)
            load(1, 1)
            load(2, 2)
            load(3, 3)
            for r in range(ROWS):
                sp.dma_start(scratch[:, r, :, :], rpb[:, :, 7 - r:15 - r]).then_inc(rows_in, 16)
            for g in range(4):
                with sp.Fori(4 * g + 1, 4 * g + 5) as i:
                    for s in range(4):
                        load(4 * i + s, 4 + s, i - 1)
                sp.wait_ge(rows_in, 16 * ROWS)
                sp.wait_ge(masks, 1)
                for c in range(4 * g, 4 * g + 4):
                    for blk in (0, 1, 3):
                        col = WIN * blk + c
                        start = min(max(col - WIN // 2, 0), GW - WIN)
                        at, first = start - KEYS[blk][0], start - col + WIN - 1
                        dst = bias[8 * c:8 * c + 8, :, BIAS_AT[blk] + 8 * at:BIAS_AT[blk] + 8 * at + 128]
                        src = scratch[:, :, first:first + WIN, :].rearrange("h r c k -> r h (c k)")
                        sp.dma_start(dst, src).then_inc(bias_in, 16)
            with sp.Fori(17, U_ATT // 4) as i:
                for s in range(4):
                    load(4 * i + s, 4 + s, i - 1)
            with sp.Fori(0, KT) as i:
                for s in range(3):
                    load(3 * i + (U_ATT + s), U_ATT + s, i, 3)
            with sp.Fori(0, (U_END - U_WO) // 4) as i:
                for s in range(4):
                    load(4 * i + (U_WO + s), U_WO + s, i)
            for m in range(KT):
                sp.wait_ge(out_ready, m + 1)
                sp.dma_start(out[m], zc[:, m, :]).then_inc(stored, 16)
            sp.wait_ge(stored, 16 * KT)

        @block.gpsimd
        def _(pool):
            pool.memset(ones[:], 1.0).then_inc(const_ready, 1)
            pool.memset(ident[:], 0.0).then_inc(const_ready, 1)
            pool.wait_ge(const_ready, 2)
            pool.affine_select(out=ident[:], in_=ident[:], compare_op=ALU.not_equal, fill=1.0, base=0,
                               pattern=[[-1, P]], channel_multiplier=1).then_inc(const_ready, 1)
            for m in range(KT):
                pool.wait_ge(x_in[m], 16)
                pool.tensor_tensor(zc[:, m, :], xs[:, m, :], xs[:, m, :], ALU.mult).then_inc(sq_done, 1)
            pool.memset(zp, 0.0).then_inc(pad_zero, 1)
            pool.memset(bias[:], MASKED).then_inc(masks, 1)

            def sum_squares(n):
                pool.wait_ge(ssq_done, n)
                if n == 3:
                    pool.wait_ge(s_free, HEADS)
                pool.memset(ssq, 0.0).then_inc(ssq_zero, 1)
                pool.wait_ge(ssq_zero, n)
                for m in range(KT if n < 4 else KT - 1):
                    pool.wait_ge(sq_done, KT * n + m + 1)
                    if m:
                        pool.wait_ge(ssq_added, adds_before(n) + m)
                    pool.tensor_tensor(ssq, ssq, sq[m % 2], ALU.add).then_inc(ssq_added, 1)

            def copy_bias(par_, head):
                pool.tensor_copy(head_bias[par_], bias[:, bass.ds(head, 1), :].rearrange("p a k -> p (a k)")
                                 ).then_inc(bias_ready, 1)

            for n in range(1, 5):
                sum_squares(n)
                if n == 2:
                    pool.wait_ge(ssq_done, 3)
                    pool.wait_ge(bias_in, 16 * 3 * WIN)
                    copy_bias(0, 0)
                    copy_bias(1, 1)
                    with pool.Fori(1, KT) as j:
                        for par_ in range(2):
                            pool.wait_ge(s_free, 2 * j)
                            copy_bias(par_, 2 * j + par_)

        def mlp_start(n):
            return U_MLP0 if n == 0 else U_MLP1

        def h_before(n):
            return KT if n == 0 else KT * (1 + CHUNKS + 1)

        @block.tensor
        def _(pe):
            def product(u, slot, bank, hi, lo, ready=None, free=3, ks=range(KT), pieces=False):
                if not pieces:
                    pe.wait_ge(w_split, u + 1)
                if free is not None:
                    pe.wait_ge(taken, u - free)
                for k in ks:
                    if pieces and k % 2 == 0:
                        if k < KT - 2:
                            pe.wait_ge(piece_split, k // 2 + 1)
                        else:
                            pe.wait_ge(w_split, 1)
                    if ready is not None:
                        pe.wait_ge(ready[0], ready[1] + (k + 1))
                    nc.tensor.matmul(dense[bank][:], w_h[slot][:, k, :], hi[:, k, :], start=k == 0, stop=False)
                    nc.tensor.matmul(dense[bank][:], w_h[slot][:, k, :], lo[:, k, :], start=False, stop=False)
                    last = nc.tensor.matmul(dense[bank][:], w_l[slot][:, k, :], hi[:, k, :], start=False,
                                            stop=k == KT - 1)
                if KT - 1 in ks:
                    last.then_inc(unit_done, 1)

            def sum_over_features(n):
                pe.wait_ge(ssq_added, adds_before(n + 1))
                for t in range(4):
                    last = nc.tensor.matmul(sums[:, t:t + 1], ssq[:, P * t:P * t + P], ones[:, 0:1],
                                            start=True, stop=True)
                last.then_inc(ssq_done, 1)

            def spread_rstd(n):
                pe.wait_ge(diag_ready, n + 1)
                nc.tensor.matmul(spread[:], ones[:], diag[:], start=True, stop=True).then_inc(spread_done, 1)

            def products(first, count, hi, lo, ready=None, norm=None, start=0):
                if norm is not None:
                    product(first, 0, 0, hi, lo, ready)
                    sum_over_features(norm)
                    product(first + 1, 1, 1, hi, lo)
                    spread_rstd(norm)
                    product(first + 2, 2, 2, hi, lo)
                    product(first + 3, 3, 3, hi, lo)
                    start = 1
                with pe.Fori(start, count // 4) as i:
                    for s in range(4):
                        product(first + 4 * i + s, s, s, hi, lo, ready if s == 0 else None)

            pe.wait_ge(const_ready, 3)
            for _ in range(11):
                nc.tensor.matmul(bank[5][:, 0:P], ones[:], ident[:], start=True, stop=True)
            product(0, 0, 0, a_h, a_l, (a_ready, 0), None, pieces=True)
            product(1, 1, 1, a_h, a_l, None, None)
            sum_over_features(0)
            product(2, 2, 2, a_h, a_l, None, None)
            spread_rstd(0)
            product(3, 3, 3, a_h, a_l, None, None)
            products(U_CV, 2 * KT, a_h, a_l, start=1)
            products(U_B, KT, a_h, a_l)
            products(U_OUT, KT, h_h, h_l, (h_ready, 0))

            def mlp(n, norm):
                def chunk(c, first=None):
                    u = mlp_start(n) + 2 * KT * c
                    products(u, KT, a_h, a_l, (a_ready, KT * norm) if first is not None else None, first)
                    products(u + KT, KT, h_h, h_l, (h_ready, h_before(n) + KT * c))

                chunk(0, norm)
                with pe.Fori(1, CHUNKS) as c:
                    chunk(c)

            mlp(0, 1)

            def scores(half, pair):
                if half == 0:
                    pe.wait_ge(taken, 3 * pair + (U_ATT + 3))
                pe.wait_ge(s_free, 2 * pair + half)
                for n, b in enumerate(HALVES[half]):
                    c0, nk = KEYS[b]
                    for par_ in range(2):
                        rows = slice(HD * par_, HD * par_ + HD)
                        last = nc.tensor.matmul(score[par_][:, score_at(half, n)], qT[rows, P * b:P * b + P],
                                                kT[rows, ROWS * c0:ROWS * (c0 + nk)], start=True, stop=True)
                last.then_inc(s_done, 1)

            def transposes(half, pair):
                pe.wait_ge(p_ready, 2 * pair + (half + 1))
                pe.wait_ge(pt_ready, 2 * pair + half)
                pe.wait_ge(pt_ready_o, 2 * pair + half)
                for par_ in range(2):
                    for n, b in enumerate(HALVES[half]):
                        at = prob_at(half, par_, n).start
                        for c, (_, width) in enumerate(CHUNKS_OF[b]):
                            t = 2 * n + c
                            last = nc.tensor.transpose(tposed[par_][0:width, P * t:P * t + P],
                                                       prob[half][:, at + P * c:at + P * c + width], ident[:])
                last.then_inc(t_done, 1)

            def values(half, pair):
                pe.wait_ge(pt_ready, 2 * pair + (half + 1))
                pe.wait_ge(pt_ready_o, 2 * pair + (half + 1))
                if half == 0:
                    pe.wait_ge(v_ready, pair + 1)
                for n, b in enumerate(HALVES[half]):
                    for c in range(2):
                        for par_ in range(2):
                            rows = slice(HD * par_, HD * par_ + HD)
                            at = 512 * par_ + P * (2 * n + c)
                            last = nc.tensor.matmul(attn_out[rows, P * b:P * b + P], v_sb[:, 2 * b + c, rows],
                                                    probT[half][:, at:at + P], start=c == 0, stop=c == 1)
                last.then_inc(pv_done, 1)

            def value_transposes(pair):
                pe.wait_ge(taken, 3 * pair + (U_ATT + 1))
                pe.wait_ge(h_ready, pair + KT * (1 + CHUNKS))
                for c in range(2):
                    for b in range(4):
                        at, width = CHUNKS_OF[b][c]
                        last = nc.tensor.transpose(vtr[c][0:width, P * b:P * b + P], vT[:, at:at + width], ident[:])
                last.then_inc(vtr_done, 1)

            attn_tiles = (h_ready, KT * (1 + CHUNKS))

            def pair_step(pair, u):
                product(u, 0, 0, a_h, a_l, None, 0)
                value_transposes(pair)
                scores(0, pair)
                product(u + 1, 1, 1, a_h, a_l, None, 2)
                scores(1, pair)
                transposes(0, pair)
                product(u + 2, 2, 0, a_h, a_l, None, 1)
                transposes(1, pair)
                values(0, pair)
                values(1, pair)

            def last_pair(pair):
                def part(s, ks):
                    product(U_WO + s, s, s, h_h, h_l, attn_tiles, None, ks)

                pe.wait_ge(taken, U_WO)
                part(0, range(3))
                value_transposes(pair)
                scores(0, pair)
                part(0, range(3, KT - 1))
                scores(1, pair)
                part(1, range(2))
                transposes(0, pair)
                part(1, range(2, KT - 1))
                pe.wait_ge(s_free, 2 * pair + 2)
                part(2, range(2))
                transposes(1, pair)
                values(0, pair)
                part(2, range(2, 4))
                values(1, pair)
                part(2, range(4, KT - 1))

            product(U_ATT, 0, 0, a_h, a_l, (a_ready, 2 * KT))
            sum_over_features(2)
            product(U_ATT + 1, 1, 1, a_h, a_l)
            spread_rstd(2)
            product(U_ATT + 2, 2, 2, a_h, a_l)
            pe.wait_ge(banks_zero, 3)
            with pe.Fori(0, KT - 1) as j:
                pair_step(j, 3 * j + (U_ATT + 3))
            last_pair(KT - 1)
            for s in range(3):
                product(U_WO + s, s, s, h_h, h_l, attn_tiles, None, [KT - 1])
            product(U_WO + 3, 3, 3, h_h, h_l)
            products(U_WO, KT, h_h, h_l, start=1)
            mlp(1, 3)
            sum_over_features(4)
            spread_rstd(4)

        @block.scalar
        def _(act):
            def split_hi(v, vc=None, i=0, per=4, idle=False):
                vc = v if vc is None else vc
                slot, count = landed(vc, i, per)
                act.wait_ge(raw_in[slot], count)
                if vc >= 3 and not idle:
                    act.wait_ge(unit_done, v - 2)
                nc.scalar.activation(w_h[slot][:], raw[slot][:], ACT.Copy).then_inc(w_hi, 1)

            def square(n, m):
                if m < 2:
                    act.wait_ge(ssq_done, n)
                else:
                    act.wait_ge(ssq_added, adds_before(n) + m - 1)
                nc.scalar.activation(sq[m % 2], xs[:, m, :], ACT.Square).then_inc(sq_done, 1)

            def split_x(n, m):
                if n:
                    act.wait_ge(taken, X_FINAL[n] + m + 1)
                else:
                    act.wait_ge(x_in[m], 16)
                if n == 4:
                    square(n, m)
                dst = a_h if n < 4 else zc
                nc.scalar.activation(dst[:, m, :], xs[:, m, :], ACT.Copy, scale=gain(n, m)).then_inc(a_hi, 1)
                if 0 < n < 4:
                    square(n, m)

            def root(n):
                act.wait_ge(var_ready, n + 1)
                nc.scalar.activation(tok[:, 1, :], tok[:, 0, :], ACT.Sqrt).then_inc(std_ready, 1)

            def second_hi(m, ready, count, func):
                act.wait_ge(ready, count)
                nc.scalar.activation(h_h[:, m, :], ev[m % 2][:], func).then_inc(h_hi, 1)

            act.wait_ge(const_ready, 1)
            nc.scalar.activation(tok[:, 4, :], ones[:, 0:4], ACT.Copy)
            act.wait_ge(par_in, 16)
            for k in range(KT):
                split_x(0, k)
                if k % 2 == 0:
                    if k == 0:
                        act.wait_ge(raw_in[0], 16)
                    nc.scalar.activation(w_h[0][:, k:k + 2, :], raw[0][:, k:k + 2, :], ACT.Copy
                                         ).then_inc(piece_hi if k < KT - 2 else w_hi, 1)
            split_hi(1)
            split_hi(2)
            root(0)
            for u in range(U_CV + 1, U_B):
                split_hi(u + AHEAD)
            for m in range(KT):
                split_hi(U_B + m + AHEAD, U_B + m + AHEAD)
                second_hi(m, y_ready, m + 1, ACT.Copy)
            for m in range(KT):
                split_hi(U_OUT + m + AHEAD, U_OUT + m + AHEAD)
                split_x(1, m)

            def mlp(n, norm):
                def chunk(c, first=False, last=False):
                    u = mlp_start(n) + 2 * KT * c
                    i = 4 * c
                    for m in range(KT):
                        vc = mlp_start(n) + m + AHEAD
                        split_hi(u + (m + AHEAD), vc, i)
                        if first and m == 0:
                            root(norm)
                        second_hi(m, taken, u + (m + 1), ACT.Square)
                    for m in range(KT):
                        vc = mlp_start(n) + KT + m + AHEAD
                        if not (last and n == 1 and m >= KT - AHEAD):
                            split_hi(u + (KT + m + AHEAD), vc, i)
                        if last:
                            split_x(norm + 1, m)

                chunk(0, first=True)
                with act.Fori(1, CHUNKS - 1) as c:
                    chunk(c)
                chunk(CHUNKS - 1, last=True)

            mlp(0, 1)

            def pair_step(pair, u):
                hi = lambda s: split_hi(u + (s + AHEAD), U_ATT + 3 + s + AHEAD, pair, 3)
                if u is not None:
                    hi(0)
                else:
                    split_hi(U_WO + AHEAD)
                act.wait_ge(vtr_done, pair + 1)
                for c in range(2):
                    last = nc.scalar.activation(v_sb.rearrange("p (b c) f -> p b c f", c=2)[:, :, c, :],
                                                vtr[c][:].rearrange("p (b f) -> p b f", b=4), ACT.Copy)
                last.then_inc(v_ready, 1)

                def exps(half):
                    act.wait_ge(neg_ready, 2 * pair + (half + 1))
                    for par_ in range(2):
                        for n in range(2):
                            t = prob[half][:, prob_at(half, par_, n)]
                            q = 2 * par_ + n
                            last = nc.scalar.activation(t, t, ACT.Exp, bias=stat[:, half, 1, q:q + 1],
                                                        accum_out=stat[:, half, 2, q:q + 1])
                    last.then_inc(exp_done, 1)

                def evacuate(half):
                    act.wait_ge(t_done, 2 * pair + (half + 1))
                    nc.scalar.activation(probT[half][:, 0:512], tposed[0][:], ACT.Copy).then_inc(pt_ready, 1)

                if u is not None:
                    hi(1)
                else:
                    split_hi(U_WO + 3, idle=True)
                exps(0)
                if u is not None:
                    hi(2)
                exps(1)
                evacuate(0)
                evacuate(1)
                act.wait_ge(pv_done, 2 * pair + 2)
                nc.scalar.activation(h_h[:, bass.ds(pair, 1), :].rearrange("p a t -> p (a t)"), attn_out[:],
                                     ACT.Copy).then_inc(h_hi, 1)

            for s in range(3):
                split_hi(U_ATT + s + AHEAD, None, 0, 3)
                if s == 0:
                    root(2)
            with act.Fori(0, KT - 1) as j:
                pair_step(j, 3 * j + (U_ATT + 3))
            pair_step(KT - 1, None)
            for m in range(KT):
                if m > 1:
                    split_hi(U_WO + m + AHEAD)
                split_x(3, m)
            mlp(1, 3)
            root(4)

        @block.vector
        def _(dve):
            steps = [0]

            def link(instruction):
                steps[0] = steps[0] + 1
                instruction.then_inc(chain, 1)
                dve.wait_ge(chain, steps[0])

            def split_lo(v, vc, i=0, per=4):
                slot, _ = landed(vc, i, per)
                dve.wait_ge(w_hi, v + 1)
                nc.vector.tensor_tensor(w_l[slot][:], raw[slot][:], w_h[slot][:].bitcast(f32),
                                        ALU.subtract).then_inc(w_split, 1)

            def split_x(n, m):
                dve.wait_ge(a_hi, KT * n + m + 1)
                nc.vector.scalar_tensor_tensor(out=a_l[:, m, :], in0=xs[:, m, :], scalar=gain(n, m),
                                               in1=a_h[:, m, :].bitcast(f32), op0=ALU.mult,
                                               op1=ALU.subtract).then_inc(a_ready, 1)

            def inverse_rms(n):
                dve.wait_ge(ssq_done, n + 1)
                nc.vector.tensor_scalar(tok[:, 0, :], sums, 1.0 / D, EPS, ALU.mult, ALU.add).then_inc(var_ready, 1)
                dve.wait_ge(std_ready, n + 1)
                link(nc.vector.reciprocal(tok[:, 2, :], tok[:, 1, :]))
                link(nc.vector.tensor_tensor(tok[:, 3, :], tok[:, 2, :], tok[:, 2, :], ALU.mult))
                link(nc.vector.scalar_tensor_tensor(out=tok[:, 3, :], in0=tok[:, 3, :], scalar=-0.5,
                                                    in1=tok[:, 0, :], op0=ALU.mult, op1=ALU.mult))
                link(nc.vector.scalar_tensor_tensor(out=tok[:, 3, :], in0=tok[:, 3, :], scalar=1.5,
                                                    in1=tok[:, 2, :], op0=ALU.add, op1=ALU.mult))
                for t in range(4):
                    last = nc.vector.tensor_scalar(diag[:, P * t:P * t + P], ident[:], tok[:, 3, t:t + 1], None,
                                                   ALU.mult)
                last.then_inc(diag_ready, 1)
                if n == 0:
                    split_lo(3, 3)
                    split_lo(4, 4)
                dve.wait_ge(spread_done, n + 1)
                if n < 4:
                    nc.vector.tensor_copy(rstd[:], spread[:]).then_inc(rstd_ready, 1)
                    dve.wait_ge(rstd_ready, n + 1)

            def scaled(u, bank, dst):
                dve.wait_ge(unit_done, u + 1)
                nc.vector.tensor_tensor(dst, dense[bank][:], rstd[:], ALU.mult).then_inc(taken, 1)

            def residual(u, bank, m):
                dve.wait_ge(unit_done, u + 1)
                nc.vector.tensor_tensor(xs[:, m, :], dense[bank][:], xs[:, m, :], ALU.add).then_inc(taken, 1)

            dve.wait_ge(par_in, 16)
            for k in range(KT):
                split_x(0, k)
                if k % 2 == 0:
                    if k < KT - 2:
                        dve.wait_ge(piece_hi, k // 2 + 1)
                    else:
                        dve.wait_ge(w_hi, 1)
                    nc.vector.tensor_tensor(w_l[0][:, k:k + 2, :], raw[0][:, k:k + 2, :],
                                            w_h[0][:, k:k + 2, :].bitcast(f32), ALU.subtract
                                            ).then_inc(piece_split if k < KT - 2 else w_split, 1)
            split_lo(1, 1)
            for m in range(2, KT):
                dve.wait_ge(sq_done, m + 1)
                if m >= 4:
                    dve.wait_ge(ssq_added, m - 3)
                nc.vector.tensor_tensor(zc[:, m % 2, :], zc[:, m % 2, :], zc[:, m, :],
                                        ALU.add).then_inc(ssq_added, 1)
            dve.wait_ge(ssq_added, KT - 2)
            nc.vector.tensor_tensor(ssq, zc[:, 0, :], zc[:, 1, :], ALU.add).then_inc(ssq_added, 1)
            split_lo(2, 2)
            inverse_rms(0)
            dve.wait_ge(pad_zero, 1)
            for m in range(KT):
                u = U_CV + 2 * m
                if m > 1:
                    split_lo(u + 2, u + 2)
                scaled(u, u % 4, ev[0][:])
                if m:
                    split_lo(u + 3, u + 3)
                scaled(u + 1, (u + 1) % 4, ev[1][:])
                dve.wait_ge(taken, u + 2)
                link(nc.vector.tensor_tensor(zp[:, 8:520], ev[0][:], ev[1][:], ALU.mult))
                nc.vector.tensor_copy(zp[:, 1:8], zp[:, 512:519])
                link(nc.vector.tensor_copy(zp[:, 520:527], zp[:, 9:16]))
                link(nc.vector.tensor_scalar(ev2[0][:], zp[:, 0:512], tap(0, m), None, ALU.mult))
                link(nc.vector.scalar_tensor_tensor(out=ev2[1][:], in0=zp[:, 8:520], scalar=tap(1, m),
                                                    in1=ev2[0][:], op0=ALU.mult, op1=ALU.add))
                link(nc.vector.scalar_tensor_tensor(out=zc[:, m, :], in0=zp[:, 16:528], scalar=tap(2, m),
                                                    in1=ev2[1][:], op0=ALU.mult, op1=ALU.add))
            for m in range(KT):
                u = U_B + m
                split_lo(u + 2, u + 2)
                scaled(u, m % 4, ev2[m % 2][:])
                dve.wait_ge(taken, u + 1)
                nc.vector.tensor_tensor(ev[m % 2][:], ev2[m % 2][:], zc[:, m, :], ALU.mult).then_inc(y_ready, 1)
                dve.wait_ge(y_ready, m + 1)
                dve.wait_ge(h_hi, m + 1)
                nc.vector.tensor_tensor(h_l[:, m, :], ev[m % 2][:], h_h[:, m, :].bitcast(f32),
                                        ALU.subtract).then_inc(h_ready, 1)
            for m in range(KT):
                u = U_OUT + m
                split_lo(u + 2, u + 2)
                residual(u, m % 4, m)
                split_x(1, m)

            def mlp(n, norm):
                def chunk(c, first=False, last=False):
                    u = mlp_start(n) + 2 * KT * c
                    i = 4 * c
                    for m in range(KT):
                        split_lo(u + (m + AHEAD), mlp_start(n) + m + AHEAD, i)
                        if first and m == 0:
                            inverse_rms(norm)
                        tile = h_before(n) + KT * c + (m + 1)
                        dve.wait_ge(unit_done, u + (m + 1))
                        nc.vector.scalar_tensor_tensor(out=ev[m % 2][:], in0=dense[m % 4][:], scalar=0.0,
                                                       in1=rstd[:], op0=ALU.max, op1=ALU.mult).then_inc(taken, 1)
                        dve.wait_ge(taken, u + (m + 1))
                        nc.vector.tensor_tensor(ev2[m % 2][:], ev[m % 2][:], ev[m % 2][:],
                                                ALU.mult).then_inc(square_ready, 1)
                        dve.wait_ge(square_ready, tile - (KT if n == 0 else 2 * KT))
                        dve.wait_ge(h_hi, tile)
                        nc.vector.tensor_tensor(h_l[:, m, :], ev2[m % 2][:], h_h[:, m, :].bitcast(f32),
                                                ALU.subtract).then_inc(h_ready, 1)
                    for m in range(KT):
                        if not (last and n == 1 and m >= KT - AHEAD):
                            split_lo(u + (KT + m + AHEAD), mlp_start(n) + KT + m + AHEAD, i)
                        residual(u + (KT + m), m % 4, m)
                        if last and norm < 3:
                            split_x(norm + 1, m)

                chunk(0, first=True)
                with dve.Fori(1, CHUNKS - 1) as c:
                    chunk(c)
                chunk(CHUNKS - 1, last=True)

            for b in tposed:
                nc.vector.memset(b[:], 0.0).then_inc(banks_zero, 1)
            mlp(0, 1)

            def soft_scores(half, pair):
                done = 2 * pair + (half + 1)
                dve.wait_ge(s_done, done)
                dve.wait_ge(bias_ready, 2 * pair + 2)
                nc.vector.memset(stat[:, half, 2, :], 0.0)
                for par_ in range(2):
                    for n, b in enumerate(HALVES[half]):
                        q = 2 * par_ + n
                        last = nc.vector.tensor_tensor_reduce(
                            out=prob[half][:, prob_at(half, par_, n)], in0=score[par_][:, score_at(half, n)],
                            in1=head_bias[par_][:, BIAS_AT[b]:BIAS_AT[b] + ROWS * KEYS[b][1]],
                            scale=1.0, scalar=-3e38, op0=ALU.add, op1=ALU.max,
                            accum_out=stat[:, half, 0, q:q + 1])
                last.then_inc(s_free, 1)
                dve.wait_ge(s_free, done)
                nc.vector.tensor_scalar(stat[:, half, 1, :], stat[:, half, 0, :], -1.0, None,
                                        ALU.mult).then_inc(neg_ready, 1)

            def normalise(half, pair):
                done = 2 * pair + (half + 1)
                dve.wait_ge(exp_done, done)
                nc.vector.reciprocal(stat[:, half, 3, :], stat[:, half, 2, :]).then_inc(inv_ready, 1)
                dve.wait_ge(inv_ready, done)
                for par_ in range(2):
                    for n in range(2):
                        t = prob[half][:, prob_at(half, par_, n)]
                        q = 2 * par_ + n
                        last = nc.vector.tensor_scalar(t, t, stat[:, half, 3, q:q + 1], None, ALU.mult)
                last.then_inc(p_ready, 1)

            def evacuate(half, pair):
                dve.wait_ge(t_done, 2 * pair + (half + 1))
                nc.vector.tensor_copy(probT[half][:, 512:1024], tposed[1][:]).then_inc(pt_ready_o, 1)

            def take_v(u):
                scaled(u, 0, vT[:])

            def take_q(u):
                dve.wait_ge(unit_done, u + 1)
                nc.vector.scalar_tensor_tensor(out=qT[:], in0=dense[1][:], scalar=HD ** -0.5, in1=rstd[:],
                                               op0=ALU.mult, op1=ALU.mult).then_inc(taken, 1)

            def take_k(u, bank_=0):
                scaled(u, bank_, kT[:])

            def pair_step(pair, u):
                lo = lambda s: split_lo(u + (s + AHEAD), U_ATT + 3 + s + AHEAD, pair, 3)
                if u is not None:
                    lo(0)
                    dve.wait_ge(vtr_done, pair + 1)
                    take_v(u)
                else:
                    split_lo(U_WO + AHEAD, U_WO + AHEAD)
                soft_scores(0, pair)
                if u is not None:
                    lo(1)
                else:
                    split_lo(U_WO + 3, U_WO + 3)
                normalise(0, pair)
                soft_scores(1, pair)
                if u is not None:
                    take_q(u + 1)
                    lo(2)
                normalise(1, pair)
                evacuate(0, pair)
                if u is not None:
                    take_k(u + 2)
                evacuate(1, pair)
                dve.wait_ge(h_hi, pair + (KT * (1 + CHUNKS) + 1))
                high = h_h[:, bass.ds(pair, 1), :].rearrange("p a t -> p (a t)").bitcast(f32)
                low = h_l[:, bass.ds(pair, 1), :].rearrange("p a t -> p (a t)")
                nc.vector.tensor_tensor(low, attn_out[:], high, ALU.subtract).then_inc(h_ready, 1)

            split_lo(U_ATT + 2, U_ATT + 2, 0, 3)
            inverse_rms(2)
            take_v(U_ATT)
            split_lo(U_ATT + 3, U_ATT + 3, 0, 3)
            take_q(U_ATT + 1)
            nc.vector.memset(vtr[1][:], 0.0).then_inc(banks_zero, 1)
            take_k(U_ATT + 2, 2)
            split_lo(U_ATT + 4, U_ATT + 4, 0, 3)
            with dve.Fori(0, KT - 1) as j:
                pair_step(j, 3 * j + (U_ATT + 3))
            pair_step(KT - 1, None)
            for m in range(KT):
                if m > 1:
                    split_lo(U_WO + m + AHEAD, U_WO + m + AHEAD)
                residual(U_WO + m, m % 4, m)
                split_x(3, m)
            mlp(1, 3)
            dve.wait_ge(sq_done, 5 * KT)
            dve.wait_ge(ssq_added, adds_before(5) - 1)
            nc.vector.tensor_tensor(ssq, ssq, sq[(KT - 1) % 2], ALU.add).then_inc(ssq_added, 1)
            inverse_rms(4)
            for m in range(KT):
                dve.wait_ge(a_hi, 4 * KT + m + 1)
                nc.vector.tensor_tensor(zc[:, m, :], zc[:, m, :], spread[:], ALU.mult).then_inc(out_ready, 1)


def kernel(x, norm_mix, conv_w_in, conv_w, conv_w_out, attn_w_qkv, attn_rpb, attn_w_o, norm_mlp,
           mlp_w_up, mlp_w_down, norm_final):
    import numpy as np
    import concourse.bacc as bacc
    from concourse.bass_utils import run_bass_kernel_spmd

    def units(w, rows, cols):
        block = w[P * KT * rows:P * KT * (rows + 1), P * cols:P * (cols + 1)]
        return block.reshape(KT, P, P).transpose(1, 0, 2).reshape(P, KT * P)

    w_in, w_qkv = conv_w_in[0], attn_w_qkv[0]
    order = []
    for m in range(KT):
        order += [units(w_in, 0, KT + m), units(w_in, 0, 2 * KT + m)]
    order += [units(w_in, 0, m) for m in range(KT)]
    order += [units(conv_w_out[0], 0, m) for m in range(KT)]

    def mlp_units(n):
        for c in range(CHUNKS):
            yield from (units(mlp_w_up[n], 0, KT * c + m) for m in range(KT))
            yield from (units(mlp_w_down[n], c, m) for m in range(KT))

    order += mlp_units(0)
    for j in range(KT):
        order += [units(w_qkv, 0, 2 * KT + j), units(w_qkv, 0, j), units(w_qkv, 0, KT + j)]
    order += [units(attn_w_o[0], 0, m) for m in range(KT)]
    order += mlp_units(1)
    weights = np.stack(order)

    x_t = x[0].reshape(ROWS, GW, D).transpose(2, 1, 0).reshape(KT, P, SEQ)
    vectors = [norm_mix[0], norm_mlp[0], norm_mix[1], norm_mlp[1], norm_final, *conv_w[0]]
    small = np.stack(vectors).reshape(8, KT, P).transpose(2, 0, 1).reshape(P, 8 * KT)
    arrays = {"x": x_t, "weights": weights, "small": small, "rpb": attn_rpb[0].transpose(0, 2, 1)}
    arrays = {name: np.ascontiguousarray(a) for name, a in arrays.items()}

    nc = bacc.Bacc("TRN2", target_bir_lowering=False, num_devices=1)
    args = [nc.dram_tensor(name, a.shape, mybir.dt.from_np(a.dtype), kind="ExternalInput").ap()
            for name, a in arrays.items()]
    out = nc.dram_tensor("out", (KT, P, SEQ), mybir.dt.float32, kind="ExternalOutput").ap()
    encoder(nc, *args, out)
    got = run_bass_kernel_spmd(nc, [arrays], core_ids=[0]).results[0]["out"]
    return np.ascontiguousarray(got.reshape(D, GW, ROWS).transpose(2, 1, 0).reshape(1, SEQ, D))
```
